# Optimizing a Trainium2 kernel written in Bass

```python
import jax, jax.numpy as jnp
from jax import lax
import numpy as np

D_MODEL = 2048
BATCH = 1
SEQ = 128
DEPTH = 1
DEC_BATCH = 1
DEC_SEQ = 512
PAST_LEN = 128

GRID_W = 64
MIX_WIDTH = D_MODEL
GLA_WIDTH = MIX_WIDTH // 2
POOL_WIDTH = MIX_WIDTH - GLA_WIDTH
GLA_HEADS = 4
GLA_DV = GLA_WIDTH // GLA_HEADS
GLA_DK = GLA_DV // 2
GLA_KEY_WIDTH = GLA_HEADS * GLA_DK
GLA_GATE_RANK = 16
GLA_GATE_TEMP = 16.0
GLA_CHUNK = 64
POOL_WINDOWS = (2, 4, 8, 16)
POOL_GROUPS = len(POOL_WINDOWS)
POOL_GROUP_DIM = POOL_WIDTH // POOL_GROUPS
D_FF = ((8 * D_MODEL + 2) // 3 + 255) // 256 * 256
ALPHA = (2 * DEPTH) ** 0.25
BETA = (8 * DEPTH) ** -0.25
LN_EPS = 1e-5
Q_OFF = 0
K_OFF = Q_OFF + GLA_KEY_WIDTH
V_OFF = K_OFF + GLA_KEY_WIDTH
G_OFF = V_OFF + GLA_WIDTH
AF_OFF = G_OFF + GLA_WIDTH
AB_OFF = AF_OFF + GLA_GATE_RANK
P_OFF = AB_OFF + GLA_GATE_RANK
IN_WIDTH = P_OFF + POOL_WIDTH

kernel_name = 'hymba_gla_pool_dit_step'

def layer_norm(x, g, b):
    xf = x.astype(jnp.float32)
    mu = jnp.mean(xf, axis=-1, keepdims=True)
    var = jnp.mean(jnp.square(xf - mu), axis=-1, keepdims=True)
    y = (xf - mu) * lax.rsqrt(var + LN_EPS) * g.astype(jnp.float32) + b.astype(jnp.float32)
    return y.astype(x.dtype)

def gla_chunked(q, k, v, log_a, s0):
    B, H, L, dk = q.shape
    dv = v.shape[-1]
    n = L // GLA_CHUNK
    r = lambda t: t.reshape(B, H, n, GLA_CHUNK, t.shape[-1])
    q, k, v, log_a = r(q), r(k), r(v), r(log_a)
    b = jnp.cumsum(log_a, axis=3)
    b_last = b[..., -1:, :]
    qe = q * jnp.exp(b)
    ke = k * jnp.exp(-b)
    kd = k * jnp.exp(b_last - b)
    order = jnp.tril(jnp.ones((GLA_CHUNK, GLA_CHUNK), dtype=bool))
    A = jnp.where(order, jnp.einsum('bhncd,bhnsd->bhncs', qe, ke), 0.0)
    o_intra = jnp.einsum('bhncs,bhnsv->bhncv', A, v)
    U = jnp.einsum('bhncd,bhncv->bhndv', kd, v)
    decay = jnp.exp(b_last[..., 0, :])

    def step(S, inp):
        d, u = inp
        return d[..., None] * S + u, S

    s_final, s_before = lax.scan(step, s0, (jnp.moveaxis(decay, 2, 0), jnp.moveaxis(U, 2, 0)))
    s_before = jnp.moveaxis(s_before, 0, 2)
    o = o_intra + jnp.einsum('bhncd,bhndv->bhncv', qe, s_before)
    return o.reshape(B, H, L, dv), s_final

def _window_bounds(n, w):
    idx = jnp.arange(n)
    lo = jnp.clip(idx - w // 2, 0, n)
    hi = jnp.clip(idx - w // 2 + w, 0, n)
    return lo, hi

def pool_1d(p, w):
    L = p.shape[1]
    P = jnp.concatenate([jnp.zeros_like(p[:, :1]), jnp.cumsum(p, axis=1)], axis=1)
    lo, hi = _window_bounds(L, w)
    cnt = (hi - lo).astype(p.dtype)
    return (P[:, hi] - P[:, lo]) / cnt[None, :, None] - p

def pool_2d(p, w):
    B, L, C = p.shape
    rows = L // GRID_W
    g = p.reshape(B, rows, GRID_W, C)
    P = jnp.pad(jnp.cumsum(jnp.cumsum(g, axis=1), axis=2), ((0, 0), (1, 0), (1, 0), (0, 0)))
    lr, hr = _window_bounds(rows, w)
    lc, hc = _window_bounds(GRID_W, w)
    Ph = P[:, hr]
    Pl = P[:, lr]
    s = Ph[:, :, hc] - Pl[:, :, hc] - Ph[:, :, lc] + Pl[:, :, lc]
    cnt = ((hr - lr)[:, None] * (hc - lc)[None, :]).astype(p.dtype)
    return (s / cnt[None, :, :, None] - g).reshape(B, L, C)

def mixer(h, s0_f, s0_b, on_grid, w_in, w_a2, b_a, gla_norm_g, w_pool, pool_scale, w_out):
    B, L, _ = h.shape
    f32 = jnp.float32
    z = h @ w_in
    q, k, v, g, a_f, a_b, p = jnp.split(z, [K_OFF, V_OFF, G_OFF, AF_OFF, AB_OFF, P_OFF], axis=-1)
    heads = lambda t, d: t.astype(f32).reshape(B, L, GLA_HEADS, d).transpose(0, 2, 1, 3)
    q = heads(q, GLA_DK) * (GLA_DK ** -0.5)
    k = heads(k, GLA_DK)
    v = heads(v, GLA_DV)
    log_a_f = heads(jax.nn.log_sigmoid((a_f @ w_a2[0] + b_a[0]).astype(f32)) / GLA_GATE_TEMP, GLA_DK)
    log_a_b = heads(jax.nn.log_sigmoid((a_b @ w_a2[1] + b_a[1]).astype(f32)) / GLA_GATE_TEMP, GLA_DK)
    flip = lambda t: jnp.flip(t, axis=2)
    o_f, s_f = gla_chunked(q, k, v, log_a_f, s0_f.astype(f32))
    o_b, s_b = gla_chunked(flip(q), flip(k), flip(v), flip(log_a_b), s0_b.astype(f32))
    o = (o_f + flip(o_b)).transpose(0, 2, 1, 3)
    o = o * lax.rsqrt(jnp.mean(jnp.square(o), axis=-1, keepdims=True) + LN_EPS)
    o = o * gla_norm_g.astype(f32).reshape(GLA_HEADS, GLA_DV)
    o = o.reshape(B, L, GLA_WIDTH) * jax.nn.silu(g.astype(f32))
    pf = p.astype(f32)
    pool_fn = pool_2d if on_grid else pool_1d
    pooled = jnp.stack([pool_fn(pf[..., i * POOL_GROUP_DIM:(i + 1) * POOL_GROUP_DIM], w)
                        for i, w in enumerate(POOL_WINDOWS)], axis=2)
    y_pool = jnp.einsum('blgc,gcd->blgd', pooled, w_pool).reshape(B, L, POOL_WIDTH)
    y_pool = y_pool * pool_scale.astype(f32)
    mixed = jnp.concatenate([o, y_pool], axis=-1).astype(h.dtype)
    return mixed @ w_out, s_f, s_b

def block(x, mod, s0_f, s0_b, on_grid, w_in, w_a2, b_a, gla_norm_g, w_pool, pool_scale, w_out,
          ln1_g, ln1_b, w_gu, w_down, ln2_g, ln2_b):
    sh1, sc1, g1, sh2, sc2, g2 = jnp.split(mod, 6, axis=-1)
    h = x * (1 + sc1) + sh1
    m, s_f, s_b = mixer(h, s0_f, s0_b, on_grid, w_in, w_a2, b_a, gla_norm_g, w_pool, pool_scale, w_out)
    x = layer_norm(ALPHA * x + g1 * m, ln1_g, ln1_b)
    h = x * (1 + sc2) + sh2
    gate, up = jnp.split(h @ w_gu, 2, axis=-1)
    f = (jax.nn.silu(gate) * up) @ w_down
    x = layer_norm(ALPHA * x + g2 * f, ln2_g, ln2_b)
    return x, s_f, s_b

def setup_inputs(seed: int = 0) -> dict:
    key = jax.random.key(seed)
    ks = jax.random.split(key, 22)
    nrm = lambda k, shape, s: jax.random.normal(k, shape, jnp.float32) * s
    return {
        'x_prompt': nrm(ks[0], (BATCH, SEQ, D_MODEL), 1.0),
        'x_sample': nrm(ks[1], (DEC_BATCH, DEC_SEQ, D_MODEL), 1.0),
        'state_gla': nrm(ks[2], (DEPTH, 2, DEC_BATCH, GLA_HEADS, GLA_DK, GLA_DV), 0.5),
        'c': nrm(ks[3], (DEC_BATCH, D_MODEL), 1.0),
        'c_ctx': nrm(ks[4], (D_MODEL,), 1.0),
        'ln_in_g': 1.0 + nrm(ks[5], (D_MODEL,), 0.05),
        'ln_in_b': nrm(ks[6], (D_MODEL,), 0.02),
        'w_ada': nrm(ks[7], (DEPTH, D_MODEL, 6 * D_MODEL), 0.5 * D_MODEL ** -0.5),
        'b_ada': nrm(ks[8], (DEPTH, 6 * D_MODEL), 0.02),
        'w_in': nrm(ks[9], (DEPTH, D_MODEL, IN_WIDTH), D_MODEL ** -0.5),
        'w_a2': nrm(ks[10], (DEPTH, 2, GLA_GATE_RANK, GLA_KEY_WIDTH), GLA_GATE_RANK ** -0.5),
        'b_a': nrm(ks[11], (DEPTH, 2, GLA_KEY_WIDTH), 0.5),
        'gla_norm_g': 1.0 + nrm(ks[12], (DEPTH, GLA_WIDTH), 0.05),
        'w_pool': nrm(ks[13], (DEPTH, POOL_GROUPS, POOL_GROUP_DIM, POOL_GROUP_DIM), POOL_GROUP_DIM ** -0.5),
        'pool_scale': 1.0 + nrm(ks[14], (DEPTH, POOL_WIDTH), 0.1),
        'w_out': nrm(ks[15], (DEPTH, MIX_WIDTH, D_MODEL), BETA * MIX_WIDTH ** -0.5),
        'ln1_g': 1.0 + nrm(ks[16], (DEPTH, D_MODEL), 0.05),
        'ln1_b': nrm(ks[17], (DEPTH, D_MODEL), 0.02),
        'w_gu': nrm(ks[18], (DEPTH, D_MODEL, 2 * D_FF), D_MODEL ** -0.5),
        'w_down': nrm(ks[19], (DEPTH, D_FF, D_MODEL), BETA * D_FF ** -0.5),
        'ln2_g': 1.0 + nrm(ks[20], (DEPTH, D_MODEL), 0.05),
        'ln2_b': nrm(ks[21], (DEPTH, D_MODEL), 0.02),
    }

def reference(x_prompt, x_sample, state_gla, c, c_ctx, ln_in_g, ln_in_b, w_ada, b_ada, w_in, w_a2,
              b_a, gla_norm_g, w_pool, pool_scale, w_out, ln1_g, ln1_b, w_gu, w_down, ln2_g, ln2_b):
    xp = layer_norm(x_prompt, ln_in_g, ln_in_b)
    xs = layer_norm(x_sample, ln_in_g, ln_in_b)
    zero_state = jnp.zeros((x_prompt.shape[0], GLA_HEADS, GLA_DK, GLA_DV), jnp.float32)
    states = []
    for l in range(DEPTH):
        lw = (w_in[l], w_a2[l], b_a[l], gla_norm_g[l], w_pool[l], pool_scale[l], w_out[l],
              ln1_g[l], ln1_b[l], w_gu[l], w_down[l], ln2_g[l], ln2_b[l])
        mod_ctx = jax.nn.silu(c_ctx) @ w_ada[l] + b_ada[l]
        mod_lat = (jax.nn.silu(c) @ w_ada[l] + b_ada[l])[:, None, :]
        xp, s_f, s_b = block(xp, mod_ctx, zero_state, zero_state, False, *lw)
        states.append(jnp.stack([s_f, s_b], axis=0))
        xs, _, _ = block(xs, mod_lat, state_gla[l, 0], state_gla[l, 1], True, *lw)
    y_prompt = xp
    y_sample = xs
    new_state_gla = jnp.stack(states, axis=0).astype(x_prompt.dtype)
    return (y_prompt, y_sample, new_state_gla)


_drawn_inputs = setup_inputs


def setup_inputs(seed=0):
    import zlib

    import numpy as np

    out = dict(_drawn_inputs(seed))
    spreads = {}
    factors = {'state_gla': 8.0,
     'gla_norm_g': 21.546,
     'pool_scale': 5.799,
     'ln1_b': 2.814,
     'ln2_b': 2.772}
    for name, (base, spread) in spreads.items():
        noise = np.random.default_rng([zlib.crc32(name.encode()), seed]).standard_normal(out[name].shape)
        drawn = base * np.exp(spread * noise) if base else spread * noise
        out[name] = __import__('jax').numpy.asarray(drawn.astype(out[name].dtype))
    for name, factor in factors.items():
        out[name] = (out[name] * factor).astype(out[name].dtype)
    return out
```

```python
import numpy as np

import concourse.bass as bass
from concourse import mybir

F32 = mybir.dt.float32
F32R = mybir.dt.float32r
U32 = mybir.dt.uint32
ALU = mybir.AluOpType
ACT = mybir.ActivationFunctionType

P = 128
D = 2048
KT = D // P
N_PROMPT, N_SAMPLE = 128, 512
T = N_PROMPT + N_SAMPLE
TT = T // P
HALF = T // 2
GRID_W = 64
ROWS = N_SAMPLE // GRID_W
HEADS, DK, DV = 4, 128, 256
KEYW = HEADS * DK
RANK = 16
GATE_TEMP = 16.0
CHUNK = 64
NCH = T // CHUNK
P_CH = N_PROMPT // CHUNK
WINDOWS = (2, 4, 8, 16)
GROUPW = 256
D_FF = 5632
FB = D_FF // P
ALPHA = 2.0 ** 0.25
EPS = 1e-5
UNIT = 2048
N_IN = 33
N_OUT = 16
SC, SH = 0, 1
V_OFF, G_OFF, A_OFF, P_OFF = 1024, 2048, 3072, 3104
K_ARR = 2 * RANK + 1



def unit_plan():
    plan = [("a", 0, 0, A_OFF)]

    def head(h):
        return [("q", h, 0, h * DK), ("k", h, 0, KEYW + h * DK),
                ("v", h, 0, V_OFF + h * DV), ("v", h, 1, V_OFF + h * DV + P)]

    def gate(h):
        return [("g", h, 0, G_OFF + h * DV), ("g", h, 1, G_OFF + h * DV + P)]

    plan += head(0)
    for h in range(1, HEADS):
        plan += gate(h - 1) + head(h)
    plan += [("p", j // 2, j % 2, P_OFF + j * P) for j in range(8)]
    plan += gate(HEADS - 1)
    return plan


PLAN = unit_plan()
assert len(PLAN) == N_IN
KG_ORDER = (2, 3, 0, 1)

C_IDENT, C_TRI, C_ONES, C_IND = 0, 128, 384, 512
C_EPS = 516
C_VEC = 517
V_NORM, V_PSC, V_LNIN, V_LN1, V_BADA, V_COND = 0, 8, 16, 48, 80, 144
N_VEC = 176
C_CSIL = C_VEC + N_VEC
C_MOD = C_CSIL + 32
C_FOLD = C_MOD + 64
C_STAT = C_FOLD + 64
C_MV = C_STAT + 48
C_BL = C_MV + 40
C_DEC = C_BL + NCH
N_PERM = C_DEC + NCH

L_Q, L_K, L_V, L_LA, L_E, L_E3 = 0, 640, 1280, 2560, 3200, 3840
L_QE, L_KE, L_ST, L_O, L_AT, L_WA = 4480, 5120, 5760, 8320, 9600, 10240
L_PA, L_PB, L_PC, L_POOLED, L_RC, L_WP, L_STAGE = 10496, 11280, 11920, 12560, 13840, 14480, 14992
PAD = 8
PROW = GRID_W + 2 * PAD
PPR = N_PROMPT + 2 * PAD
S_XT, S_X = 0, 10240
W_U, W_MIX, W_STAT = 0, 10496, 16128
W_GATE = (13056, 10496)
N_VECB, N_HT = 10240, 14336
F_ACC, F_SIL, F_HF = 0, 10240, 11520
E_GATE, E_X = 10240, 14336
LOW = 16384
H_ACC, H_RING, H_ROW = 0, 1024, 2560
HIGH = 3072
ADA_SLOTS = 3
ADA = [(2, "row", 0), (4, "col", SC), (3, "col", SH), (5, "row", 1)]
X_LOADS = (3, 7, 14, 22)
X_TURNS = (3, 7, 11, 19, 23)
N_ADA_Q = 4


def make_schedule():
    steps = []
    for n, (kind, h, j, _) in enumerate(PLAN):
        gap = [[], [], [], []]
        steps.append([n, gap])

    def put(n, quarter, *items):
        n, quarter = n + quarter // 4, quarter % 4
        steps[n][1][quarter].extend(items)

    where = {(k, h, j): n for n, (k, h, j, _) in enumerate(PLAN)}
    for h in range(HEADS):
        after_k = 4 * (where["k", h, 0] + 1)
        for at, item in ((1, ("wa", h, 0)), (2, ("state", h, 0)), (4, ("gate", h, 0)),
                         (5, ("vT", h, 0)), (6, ("cum", h, 0)), (8, ("score", h, 0)),
                         (9, ("vT", h, 1)), (10, ("outer", h, 0)), (12, ("mix", h, 0)),
                         (12, ("gate", h, 1)), (14, ("state", h, 1)), (14, ("final", h, 0)),
                         (15, ("cum", h, 1)), (17, ("score", h, 1)), (20, ("outer", h, 1)),
                         (23, ("mix", h, 1)), (24, ("final", h, 1)), (25, ("square", h, 0)),
                         (26, ("norm", h, 0)), (29, ("o_store", h, 0))):
            put(0, after_k + at, item)
    for j in range(8):
        put(where["p", j // 2, j % 2], 4, ("pool", j // 2, j % 2))
    for g in range(4):
        put(where["p", g, 1], 7, ("poolmm", g, 0))
    n_ada = 3 * N_ADA_Q
    span = 4 * (N_IN - 1) - 10
    for a in range(n_ada):
        at = 4 + a * span // n_ada
        for k in range(KT):
            put(0, at + k * 8 // KT, ("ada", a, k))
        put(0, at + 9, ("adasum", a, 0))
        if ADA[a // 4][1] == "col":
            put(0, at + 10, ("adacol", a, 0))
        else:
            put(0, at + 11, ("row_store", a, 0))
    flat = []
    for n, gap in steps:
        for quarter in range(4):
            flat.append(("main", n, quarter))
            if quarter == 3:
                flat.append(("evac", n, 0))
            flat.extend(gap[quarter])
    return flat


def add_pairs(flat, fills):
    used = [0, 0]
    need = {"gate": "A", "cum": "B", "score": "AB", "outer": "ABA", "mix": "AB", "norm": "A",
            "vT": "B", "poolmm": "AB", "adasum": "B", "adacol": "A"}
    out = []
    for kind, a, b in flat:
        uses = []
        for c in need.get(kind, ""):
            x = "AB".index(c)
            uses.append((x, used[x]))
            used[x] += 1
        out.append((kind, a, b, uses))
    fills.extend(used)
    return out


FILLS = []
SCHEDULE = add_pairs(make_schedule(), FILLS)
USES = {(kind, a, b): uses for kind, a, b, uses in SCHEDULE}


def stage_uses():
    out = []
    for kind, a, b, _ in SCHEDULE:
        if kind == "evac" and PLAN[a][0] in "vg":
            out.append((PLAN[a][0],) + PLAN[a][1:3])
        if kind == "poolmm":
            out += [("y", a, 0), ("y", a, 1)]
    return out


STAGE = stage_uses()
STAGE_AT = {key: i for i, key in enumerate(STAGE)}


def spills_before(i, slot):
    return sum(1 for k in range(i) if k % 2 == slot and STAGE[k][0] != "v")


def chunk_order(d):
    pr, sa = list(range(P_CH)), list(range(P_CH, NCH))
    return (pr, sa) if d == 0 else (pr[::-1], sa[::-1])


def state_slot(d):
    pr, sa = chunk_order(d)
    slots = {pr[1]: 0}
    slots.update({c: 1 + j for j, c in enumerate(sa)})
    return slots


def outer_col(i):
    return (i % 2) * 512 + (i % 4 // 2) * 256


FINAL = 9


def backbone(nc, x_all, state_gla, w_ada, w_in_b, wa2, w_pool_l, w_out, w_gu_b, w_down, consts,
             vecs, rcnt, rows, y_all, new_state):
    x1_d = nc.dram_tensor("x1_scratch", (TT, P, D), F32, kind="Internal").ap()
    mix_d = nc.dram_tensor("mixed_scratch", (KT, P, T), F32, kind="Internal").ap()
    gs_d = nc.dram_tensor("silu_g_scratch", (8, P, T), F32, kind="Internal").ap()
    mod_d = nc.dram_tensor("gates_scratch", (2, 2, D), F32, kind="Internal").ap()

    x_t = x_all.rearrange("(t p) d -> t p d", p=P)
    y_t = y_all.rearrange("(t p) d -> t p d", p=P)
    w_ada_v = w_ada.rearrange("(k p) (g q c) -> g q k p c", p=P, g=6, q=4)
    w_ada_g = w_ada.rearrange("(k p) (g c) -> g k p c", p=P, g=6)
    w_out_v = w_out.rearrange("(kg k p) (nb c) -> nb kg p k c", kg=4, k=4, p=P, nb=4)
    w_down_v = w_down.rearrange("(b p) c -> b p c", p=P)

    perm = nc.alloc_sbuf_tensor("perm", [P, N_PERM], F32)
    x_hi = nc.alloc_sbuf_tensor("x_hi", [P, KT, T], F32R)
    x_lo = nc.alloc_sbuf_tensor("x_lo", [P, KT, T], F32R)
    raw_w = nc.alloc_sbuf_tensor("raw_w", [P, 2, UNIT], F32)
    w_hi = nc.alloc_sbuf_tensor("w_hi", [P, 2, UNIT], F32R)
    w_lo = nc.alloc_sbuf_tensor("w_lo", [P, 2, UNIT], F32R)
    low = nc.alloc_sbuf_tensor("low", [P, LOW], F32)
    with nc.sbuf_tensor("high", [P, HIGH], F32) as high:
        pass
    hid = nc.alloc_sbuf_tensor("hid", [P, 2, 2, T], F32R)
    ps = nc.alloc_psum_tensor("ps", [P, 8, 512], F32)
    flat_ps = ps[:, :, :].rearrange("p b c -> p (b c)")

    def sem(name):
        return nc.alloc_semaphore(name)

    def cols(c, n):
        return perm[:, c:c + n]

    def lo(c, n):
        return low[:, c:c + n]

    def pair(x, n=T):
        return flat_ps[:, (4 + 2 * x) * 512:(4 + 2 * x) * 512 + n]

    def tiles(ap, w=P):
        return ap.rearrange("p (t c) -> p t c", c=w)

    ident = cols(C_IDENT, P)
    ones = cols(C_ONES, P)
    vec = lambda off, n: cols(C_VEC + off, n)
    cond_silu = cols(C_CSIL, 32).rearrange("p (k c) -> p k c", c=2)
    mod_col = cols(C_MOD, 64).rearrange("p (s k c) -> p s k c", s=2, c=2)
    fold = cols(C_FOLD, 64).rearrange("p (s k c) -> p s k c", s=2, c=2)
    b_ada_col = vec(V_BADA, 64).rearrange("p (s k) -> p s k", s=4)

    def tri(d):
        return cols(C_TRI + d * P, P)

    def mv(t, i, n=1):
        return cols(C_MV + 4 * t + i, n)

    raw_half = raw_w[:, :, :].rearrange("p s (h c) -> p (s h) c", h=2)
    xT = lo(S_XT, 10240).rearrange("p (k c) -> p k c", k=KT)
    u_acc = lo(W_U, 10240).rearrange("p (t c) -> p t c", t=TT)

    consts_in = sem("consts_in")
    x_in = [sem(f"x_in{i}") for i in range(3)]
    ln_rows_in = sem("ln_rows_in")
    raw_in = [sem("raw_in0"), sem("raw_in1")]
    cond_ready = sem("cond_ready")
    mod_used = sem("mod_used")
    mod_rows = sem("mod_rows")
    mod_turned = sem("mod_turned")
    mod_cols = sem("mod_cols")
    moments = sem("moments")
    normed = sem("normed")
    turned = sem("turned")
    turned_out = sem("turned_out")
    half_in = [sem(f"half_in{i}") for i in range(4)]
    x_normed = sem("x_normed")
    folded = sem("folded")
    h_tmp = sem("h_tmp")
    h_split = sem("h_split")
    w_hi_done = sem("w_hi_done")
    ffn_hi = sem("ffn_hi")
    split_done = sem("split_done")
    unit_used = sem("unit_used")
    zin_evac = sem("zin_evac")
    filled = [sem("pair_a_filled"), sem("pair_b_filled")]
    drained = [sem("pair_a_drained"), sem("pair_b_drained")]
    ones_row = sem("ones_row")
    wa_in = sem("wa_in")
    gate_split = sem("gate_split")
    softplus = sem("softplus")
    la_ready = sem("la_ready")
    bdiff = sem("bdiff")
    expb = sem("expb")
    expd = sem("expd")
    qe_done = sem("qe_done")
    kd_done = sem("kd_done")
    ke_done = sem("ke_done")
    state_in = sem("state_in")
    scanned = sem("scanned")
    final_state = sem("final_state")
    state_out = sem("state_out")
    squared = sem("squared")
    rms_done = sem("rms_done")
    o_normed = sem("o_normed")
    o_out = sem("o_out")
    staged = sem("staged")
    spilled = [sem("spilled0"), sem("spilled1")]
    pads_zero = sem("pads_zero")
    pa_ready = sem("pa_ready")
    pooled = sem("pooled")
    pool_in = sem("pool_in")
    ada_in = [sem(f"ada_in{i}") for i in range(ADA_SLOTS)]
    ada_used = sem("ada_used")
    row_mm = sem("row_mm")
    ada_row = sem("ada_row")
    row_out = sem("row_out")
    mix_in = [sem("mix_in0"), sem("mix_in1")]
    mix_split = sem("mix_split")
    u_in = sem("u_in")
    res_gain = sem("res_gain")
    gate_in = [sem("gate_in0"), sem("gate_in1")]
    out_filled = sem("out_filled")
    out_evac = sem("out_evac")
    ln1_moments = sem("ln1_moments")
    x1_done = sem("x1_done")
    x1_out = sem("x1_out")
    turned2 = sem("turned2")
    h2_tmp = sem("h2_tmp")
    h2_split = sem("h2_split")
    silu_done = sem("silu_done")
    gated = sem("gated")
    hid_hi = sem("hid_hi")
    hid_ready = sem("hid_ready")
    down_tile = sem("down_tile")
    down_evac = sem("down_evac")
    tail_rows_in = sem("tail_rows_in")
    x1_in = sem("x1_in")
    gates2 = sem("gates2")
    y_sum = sem("y_sum")
    y_norm = sem("y_norm")
    y_done = sem("y_done")
    y_out = sem("y_out")
    dve_step = sem("dve_step")
    act_step = sem("act_step")
    block = nc.Block().__enter__()

    OUT_ACC = TT * 4
    FU = N_IN + N_OUT
    PEEL = 5

    def scan_index(h, d):
        return 2 * h + d

    @block.sync
    def _(sp):
        sp.dma_start(perm[:, 0:C_VEC], consts).then_inc(consts_in, 16)
        sp.dma_start(vec(0, N_VEC), vecs).then_inc(consts_in, 16)

        def load_x(t):
            if t >= 3:
                sp.wait_ge(turned, 4 * (t - 2))
            sp.dma_start(lo(S_X + (t % 3) * D, D), x_t[t]).then_inc(x_in[t % 3], 16)

        def load_mod(r):
            g = 1 if r < 2 * KT else 0
            if r >= 4:
                sp.wait_ge(mod_used, r - 3)
            sp.dma_start(raw_half[:, r % 4, :],
                         w_ada_g[g, (r // 2) % KT][:, 1024 * (r % 2):1024 * (r % 2) + 1024]).then_inc(
                half_in[r % 4], 16)

        load_x(0)
        for r in range(4 * KT):
            load_mod(r)
            if r in X_LOADS:
                load_x(1 + X_LOADS.index(r))

        def load_unit(u, src):
            if u < 2:
                sp.wait_ge(mod_used, 4 * KT - 2 + 2 * u)
            else:
                sp.wait_ge(split_done, u - 1)
            sp.dma_start(raw_w[:, u % 2, :], src).then_inc(raw_in[u % 2], 16)

        def load_ada(i):
            a, k, slot = i // KT, i % KT, i % ADA_SLOTS
            if i < ADA_SLOTS:
                sp.wait_ge(h_split, KT)
            else:
                sp.wait_ge(ada_used, i - ADA_SLOTS + 1)
            sp.dma_start(high[:, H_RING + 512 * slot:H_RING + 512 * slot + 512],
                         w_ada_v[ADA[a // 4][0], a % 4, k]).then_inc(ada_in[slot], 16)

        load_unit(0, w_in_b[0])
        load_unit(1, w_in_b[1])
        load_unit(2, w_in_b[2])
        for kind, a, b, uses in SCHEDULE:
            g = scan_index(a, b)
            if kind == "main" and b == 2 and a + 3 < N_IN:
                load_unit(a + 3, w_in_b[a + 3])
            elif kind == "main" and b == 2 and a + 3 < N_IN + 2:
                load_unit(a + 3, w_out_v[0, KG_ORDER[a + 3 - N_IN]])
            elif kind == "ada":
                i = KT * a + b
                if i == 0:
                    for j in range(ADA_SLOTS):
                        load_ada(j)
                if i + ADA_SLOTS < KT * 3 * N_ADA_Q:
                    load_ada(i + ADA_SLOTS)
            elif kind == "row_store":
                x, k = USES["adasum", a, 0][0]
                sp.wait_ge(drained[x], k + 1)
                sp.dma_start(mod_d[ADA[a // 4][2], :, (a % 4) * 512:(a % 4) * 512 + 512],
                             high[0:2, H_ROW:H_ROW + 512]).then_inc(row_out, 16)
            elif kind == "wa":
                if a:
                    x, k = USES["gate", a - 1, 1][0]
                    sp.wait_ge(filled[x], k + 1)
                sp.dma_start(low[0:K_ARR, L_WA:L_WA + 256].rearrange("p (d c) -> p d c", d=2),
                             wa2[:, :, a * DK:(a + 1) * DK]).then_inc(wa_in, 16)
            elif kind == "state":
                if g:
                    for x, k in USES["mix", (g - 1) // 2, (g - 1) % 2]:
                        sp.wait_ge(filled[x], k + 1)
                sp.dma_start(lo(L_ST + 256, 256), state_gla[b, a]).then_inc(state_in, 16)
            elif kind == "final":
                sp.wait_ge(final_state, g + 1)
                sp.dma_start(new_state[b, a], lo(L_ST + FINAL * 256, 256)).then_inc(state_out, 16)
            elif kind == "o_store":
                sp.wait_ge(o_normed, 2 * a + 2)
                sp.dma_start(mix_d[2 * a:2 * a + 2].rearrange("j p c -> p j c"),
                             lo(L_O, 2 * T).rearrange("p (j c) -> p j c", j=2)).then_inc(o_out, 16)
            elif kind == "main" and b == 3 and PLAN[a][0] == "p" and PLAN[a][2] == 0:
                g = PLAN[a][1]
                if g:
                    for x, k in USES["poolmm", g - 1, 0]:
                        sp.wait_ge(filled[x], k + 1)
                sp.dma_start(lo(L_RC, T), rcnt[g:g + 1, :].to_broadcast([P, T])).then_inc(pool_in, 16)
                sp.dma_start(lo(L_WP, 512).rearrange("p (c d) -> p c d", c=2),
                             w_pool_l[g]).then_inc(pool_in, 16)

        def load_mix(i):
            kt = KG_ORDER[i // 4] * 4 + i % 4
            base = W_MIX + (i % 2) * 2 * T
            if i >= 2:
                sp.wait_ge(mix_split, i - 1)
            sp.dma_start(lo(base, T), mix_d[kt]).then_inc(mix_in[i % 2], 16)
            if kt < 8:
                sp.dma_start(lo(base + T, T), gs_d[kt]).then_inc(mix_in[i % 2], 16)

        def load_gates(nb):
            base = W_GATE[nb % 2]
            if nb >= 2:
                sp.wait_ge(out_evac, TT * (nb - 1))
            c = slice(nb * 512, nb * 512 + 512)
            for i in range(2):
                sp.dma_start(lo(base + 512 * i, 512),
                             mod_d[0, i:i + 1, c].to_broadcast([P, 512])).then_inc(gate_in[nb % 2], 16)
            for i, row in enumerate((6, 0, 1)):
                sp.dma_start(lo(base + 1024 + 512 * i, 512),
                             rows[row:row + 1, c].to_broadcast([P, 512])).then_inc(gate_in[nb % 2], 16)

        n_out = spills_before(len(STAGE), 0), spills_before(len(STAGE), 1)
        sp.wait_ge(pooled, 8)
        for x, k in USES["poolmm", 3, 0]:
            sp.wait_ge(filled[x], k + 1)
        for x in range(2):
            sp.wait_ge(spilled[x], 16 * n_out[x])
        sp.wait_ge(o_out, 16 * HEADS)
        sp.wait_ge(row_out, 16 * 4)
        sp.wait_ge(state_out, 16 * 2 * HEADS)
        load_mix(0)
        load_mix(1)
        for x in range(2):
            sp.wait_ge(drained[x], FILLS[x])
        sp.dma_start(u_acc, x_all.rearrange("(t p) c -> p t c", p=P)).then_inc(u_in, 16)
        load_gates(0)
        for i in range(2, N_OUT):
            for m in range(4 * i - 6, min(4 * i - 2, KT)):
                load_mix(m)
            load_unit(N_IN + i, w_out_v[i // 4, KG_ORDER[i % 4]])
            if i == 5:
                sp.wait_ge(mix_split, KT)
            if i in (5, 7, 11):
                load_gates((i + 1) // 4 if i > 5 else 1)
        for i in range(4):
            load_unit(FU + i, w_gu_b[i])
            if i == 1:
                sp.wait_ge(out_evac, OUT_ACC)
                sp.dma_start(lo(N_VECB, D), rows[2:3, :].to_broadcast([P, D])).then_inc(ln_rows_in, 16)
                sp.dma_start(lo(N_VECB + D, D), rows[3:4, :].to_broadcast([P, D])).then_inc(ln_rows_in, 16)
        for t in range(TT):
            sp.wait_ge(x1_done, t + 1)
            sp.dma_start(x1_d[t], u_acc[:, t, :]).then_inc(x1_out, 16)

        load_unit(FU + 4, w_down_v[0])
        with sp.Fori(1, FB // 2) as i:
            for j in range(6):
                sp.wait_ge(split_done, i * 6 + (FU + PEEL - 6 + j - 1))
                if j % 3 == 2:
                    src = w_down_v[i * 2 + (j // 3 - 1)]
                else:
                    src = w_gu_b[i * 4 + (2 * (j // 3) + j % 3)]
                sp.dma_start(raw_w[:, (FU + PEEL + j) % 2, :], src).then_inc(
                    raw_in[(FU + PEEL + j) % 2], 16)
        last = FU + PEEL + 6 * (FB // 2 - 1)
        load_unit(last, w_down_v[FB - 1])

        sp.wait_ge(split_done, last + 1)
        sp.dma_start(raw_w[:, 0, :], rows[4:5, :].to_broadcast([P, D])).then_inc(tail_rows_in, 16)
        sp.dma_start(raw_w[:, 1, :], rows[5:6, :].to_broadcast([P, D])).then_inc(tail_rows_in, 16)
        sp.wait_ge(row_out, 16 * 8)
        sp.wait_ge(hid_ready, FB)
        for i in range(2):
            sp.dma_start(lo(E_GATE + i * D, D),
                         mod_d[1, i:i + 1, :].to_broadcast([P, D])).then_inc(tail_rows_in, 16)
        sp.dma_start(lo(E_X, D), rows[7:8, :].to_broadcast([P, D])).then_inc(tail_rows_in, 16)
        sp.wait_ge(x1_out, 16 * TT)
        for t in range(TT):
            if t:
                sp.wait_ge(y_sum, t)
            else:
                sp.wait_ge(gates2, 1)
            sp.dma_start(lo(E_X, D), x1_d[t]).then_inc(x1_in, 16)
            if t:
                sp.wait_ge(y_done, t)
                sp.dma_start(y_t[t - 1], u_acc[:, t - 1, :]).then_inc(y_out, 16)
        sp.wait_ge(y_done, TT)
        sp.dma_start(y_t[TT - 1], u_acc[:, TT - 1, :]).then_inc(y_out, 16)
        sp.wait_ge(y_out, 16 * TT)

    @block.gpsimd
    def _(pool):
        def split(u):
            s = u % 2
            pool.wait_ge(raw_in[s], 16 * (u // 2 + 1))
            if u >= 2:
                pool.wait_ge(unit_used, u - 1)
            nc.gpsimd.tensor_scalar(w_hi[:, s, :], raw_w[:, s, :], 1.0, None,
                                    ALU.mult).then_inc(w_hi_done, 1)
            pool.wait_ge(w_hi_done, u + 1)
            nc.gpsimd.tensor_tensor(w_lo[:, s, :], raw_w[:, s, :], w_hi[:, s, :].bitcast(F32),
                                    ALU.subtract).then_inc(split_done, 1)

        split(0)
        split(1)
        pool.wait_ge(h_split, KT)
        nc.gpsimd.memset(lo(L_PA, PPR + ROWS * PROW), 0.0).then_inc(pads_zero, 1)
        pool.wait_ge(pads_zero, 1)
        nc.gpsimd.memset(low[2 * RANK:K_ARR, L_AT:L_AT + T], 1.0).then_inc(ones_row, 1)
        pool.wait_ge(ones_row, 1)
        for kind, a, b, uses in SCHEDULE:
            if kind == "main" and b == 0:
                split(a + 2)
        for u in range(N_IN + 2, FU):
            split(u)

        def split_lo(s, u):
            pool.wait_ge(ffn_hi, u + 1)
            nc.gpsimd.tensor_tensor(w_lo[:, s, :], raw_w[:, s, :], w_hi[:, s, :].bitcast(F32),
                                    ALU.subtract).then_inc(split_done, 1)

        for u in range(PEEL):
            split_lo((FU + u) % 2, u)
        with pool.Fori(1, FB // 2) as i:
            for j in range(6):
                split_lo((FU + PEEL + j) % 2, i * 6 + (PEEL - 6 + j))
        split_lo((FU + 3 * FB - 1) % 2, 3 * FB - 1)

    @block.scalar
    def _(act):
        steps = [0]

        def link(ins):
            steps[0] += 1
            ins.then_inc(act_step, 1)
            act.wait_ge(act_step, steps[0])

        act.wait_ge(consts_in, 32)
        nc.scalar.activation(cols(C_CSIL, 32), vec(V_COND, 32), ACT.Silu).then_inc(cond_ready, 1)

        def deviation(t):
            link(nc.scalar.activation(mv(t, 2), mv(t, 1), ACT.Ln, bias=cols(C_EPS, 1)))
            link(nc.scalar.activation(mv(t, 2), mv(t, 2), ACT.Exp, scale=-0.5))
            link(nc.scalar.activation(mv(t, 3), mv(t, 0), ACT.Copy, scale=mv(t, 2)))
            link(nc.scalar.activation(mv(t, 3), mv(t, 3), ACT.Copy, scale=-1.0))

        def normalise(t, tile, moments_done, n):
            act.wait_ge(moments_done, n)
            deviation(t)
            nc.scalar.activation(tile, tile, ACT.Identity, bias=mv(t, 3),
                                 scale=mv(t, 2)).then_inc(normed, 1)

        for g in range(2):
            for t in ((0, 1, 2), (3, 4))[g]:
                normalise(TT + t, lo(S_X + (t % 3) * D, D), moments, t + 1)
            for q in range(4):
                i = 4 * g + q
                act.wait_ge(mod_used, 2 * KT * (g + 1))
                if i >= 2:
                    act.wait_ge(mod_turned, i - 1)
                nc.scalar.activation(high[0:2, 2048 + 512 * (q % 2):2560 + 512 * (q % 2)],
                                     ps[0:2, q, :], ACT.Copy).then_inc(mod_rows, 1)

        for k in range(KT):
            tmp = high[:, (k % 2) * T:(k % 2) * T + T]
            if k % 4 == 0:
                act.wait_ge(folded, k // 4 + 1)
            if k >= 2:
                act.wait_ge(h_split, k - 1)
            nc.scalar.activation(tmp[:, 0:N_PROMPT], xT[:, k, 0:N_PROMPT], ACT.Identity,
                                 bias=fold[:, SH, k, 0:1], scale=fold[:, SC, k, 0:1])
            nc.scalar.activation(tmp[:, N_PROMPT:T], xT[:, k, N_PROMPT:T], ACT.Identity,
                                 bias=fold[:, SH, k, 1:2], scale=fold[:, SC, k, 1:2]).then_inc(h_tmp, 1)

        def zin(n):
            s = 2 * (n % 2)
            return ps[:, s:s + 2, 0:HALF]

        def halves(ap):
            return ap.rearrange("p (b c) -> p b c", b=2)

        def stage_slot(i):
            return lo(L_STAGE + (i % 2) * T, T)

        def stage_free(i):
            if i < 2:
                return
            key = STAGE[i - 2]
            if key[0] == "v":
                x, k = USES[("vT",) + key[1:]][0]
                act.wait_ge(filled[x], k + 1)
            else:
                act.wait_ge(spilled[i % 2], 16 * spills_before(i - 1, i % 2))

        def evac(n):
            kind, h, j, _ = PLAN[n]
            act.wait_ge(unit_used, n + 1)
            if n == 0:
                act.wait_ge(h_split, KT)
            if kind == "a":
                nc.scalar.activation(halves(low[0:2 * RANK, L_AT:L_AT + T]),
                                     ps[0:2 * RANK, 0:2, 0:HALF], ACT.Copy).then_inc(zin_evac, 1)
            elif kind in "qk":
                if h:
                    act.wait_ge(qe_done, 2 * h)
                    act.wait_ge(ke_done, 2 * h)
                dst = lo(L_Q if kind == "q" else L_K, T)
                nc.scalar.activation(halves(dst), zin(n), ACT.Copy,
                                     scale=DK ** -0.5 if kind == "q" else 1.0).then_inc(zin_evac, 1)
            elif kind == "v":
                i = STAGE_AT["v", h, j]
                stage_free(i)
                nc.scalar.activation(halves(stage_slot(i)), zin(n), ACT.Copy).then_inc(zin_evac, 1)
            elif kind == "g":
                i = STAGE_AT["g", h, j]
                stage_free(i)
                nc.scalar.activation(halves(stage_slot(i)), zin(n), ACT.Silu).then_inc(zin_evac, 1)
                act.wait_ge(zin_evac, n + 1)
                act.dma_start(gs_d[2 * h + j], stage_slot(i)).then_inc(spilled[i % 2], 16)
            else:
                act.wait_ge(pads_zero, 1)
                jj = 2 * h + j
                if jj:
                    act.wait_ge(pooled, jj)
                s = 2 * (n % 2)
                grid = lo(L_PA + PPR, ROWS * PROW).rearrange("p (r c) -> p r c", r=ROWS)
                first = (HALF - N_PROMPT) // GRID_W
                nc.scalar.activation(lo(L_PA + PAD, N_PROMPT), ps[:, s, 0:N_PROMPT], ACT.Copy)
                nc.scalar.activation(grid[:, 0:first, PAD:PAD + GRID_W],
                                     ps[:, s, N_PROMPT:HALF].rearrange("p (r c) -> p r c", c=GRID_W),
                                     ACT.Copy)
                nc.scalar.activation(grid[:, first:ROWS, PAD:PAD + GRID_W],
                                     ps[:, s + 1, 0:HALF].rearrange("p (r c) -> p r c", c=GRID_W),
                                     ACT.Copy).then_inc(zin_evac, 1)

        for kind, a, b, uses in SCHEDULE:
            g = scan_index(a, b) if kind in ("gate", "cum", "score", "outer", "mix") else 0
            if kind == "evac":
                evac(a)
            elif kind == "vT":
                x, k = uses[0]
                if a and b == 0:
                    for xx, kk in USES["mix", a - 1, 1]:
                        act.wait_ge(filled[xx], kk + 1)
                act.wait_ge(filled[x], k + 1)
                nc.scalar.activation(tiles(lo(L_V, TT * DV), DV)[:, :, b * P:(b + 1) * P],
                                     tiles(pair(x)), ACT.Copy).then_inc(drained[x], 1)
            elif kind == "gate":
                x, k = uses[0]
                e = lo(L_E, T)
                act.wait_ge(gate_split, g + 1)
                nc.scalar.activation(e, pair(x), ACT.Abs).then_inc(drained[x], 1)
                act.wait_ge(drained[x], k + 1)
                link(nc.scalar.activation(e, e, ACT.Exp, scale=-1.0))
                nc.scalar.activation(e, e, ACT.Ln, bias=1.0).then_inc(softplus, 1)
            elif kind == "cum":
                x, k = uses[0]
                act.wait_ge(bdiff, g + 1)
                nc.scalar.activation(cols(C_DEC, NCH), cols(C_BL, NCH), ACT.Exp)
                nc.scalar.activation(lo(L_E, T), pair(x), ACT.Exp).then_inc(expb, 1)
                nc.scalar.activation(lo(L_E3, T), lo(L_E3, T), ACT.Exp).then_inc(expd, 1)
                act.wait_ge(qe_done, g + 1)
                nc.scalar.activation(lo(L_E, T), pair(x), ACT.Exp,
                                     scale=-1.0).then_inc(drained[x], 1)
            elif kind == "score":
                x, k = uses[1]
                act.wait_ge(filled[x], k + 1)
                nc.scalar.activation(lo(L_LA, T), pair(x), ACT.Copy).then_inc(drained[x], 1)
            elif kind == "square":
                for x, k in USES["mix", a, 1]:
                    act.wait_ge(drained[x], k + 1)
                nc.scalar.activation(lo(L_E, 2 * T), lo(L_O, 2 * T), ACT.Square).then_inc(squared, 1)
            elif kind == "norm":
                x, k = uses[0]
                act.wait_ge(filled[x], k + 1)
                nc.scalar.activation(lo(L_LA, T), pair(x), ACT.Ln, scale=1.0 / DV,
                                     bias=cols(C_EPS, 1)).then_inc(drained[x], 1)
                act.wait_ge(drained[x], k + 1)
                nc.scalar.activation(lo(L_LA, T), lo(L_LA, T), ACT.Exp, scale=-0.5).then_inc(rms_done, 1)
            elif kind == "poolmm":
                for blk, (x, k) in enumerate(uses):
                    i = STAGE_AT["y", a, blk]
                    stage_free(i)
                    act.wait_ge(filled[x], k + 1)
                    nc.scalar.activation(stage_slot(i), pair(x), ACT.Copy,
                                         scale=vec(V_PSC + 2 * a + blk, 1)).then_inc(drained[x], 1)
                    act.wait_ge(drained[x], k + 1)
                    act.dma_start(mix_d[8 + 2 * a + blk], stage_slot(i)).then_inc(spilled[i % 2], 16)
            elif kind == "adasum":
                x, k = uses[0]
                rows_out = sum(1 for i in range(a) if ADA[i // 4][1] == "row")
                act.wait_ge(filled[x], k + 1)
                if a and ADA[(a - 1) // 4][1] == "row":
                    act.wait_ge(row_out, 16 * rows_out)
                elif a:
                    xx, kk = USES["adacol", a - 1, 0][0]
                    act.wait_ge(filled[xx], kk + 1)
                nc.scalar.activation(high[0:2, H_ROW:H_ROW + 512], pair(x, 512)[0:2, :],
                                     ACT.Copy).then_inc(drained[x], 1)

        act.wait_ge(u_in, 16)
        for t in range(TT):
            nc.scalar.activation(u_acc[:, t, :], u_acc[:, t, :], ACT.Identity, bias=mv(TT + t, 3),
                                 scale=mv(TT + t, 2)).then_inc(x_normed, 1)
        for a in range(12, 16):
            for k in range(KT):
                i = KT * a + k
                act.wait_ge(ada_used, i - ADA_SLOTS + 1)
                act.dma_start(high[:, H_RING + 512 * (i % ADA_SLOTS):H_RING + 512 * (i % ADA_SLOTS) + 512],
                              w_ada_v[ADA[3][0], a % 4, k]).then_inc(ada_in[i % ADA_SLOTS], 16)
            act.wait_ge(row_mm, a - 11)
            if a > 12:
                act.wait_ge(row_out, 16 * (a - 8))
            nc.scalar.activation(high[0:2, H_ROW:H_ROW + 512], ps[0:2, 7, :], ACT.Copy).then_inc(ada_row, 1)
            act.wait_ge(ada_row, a - 11)
            act.dma_start(mod_d[1, :, (a - 12) * 512:(a - 11) * 512],
                          high[0:2, H_ROW:H_ROW + 512]).then_inc(row_out, 16)

        def split_hi(s, u, uses):
            act.wait_ge(raw_in[s], uses * 16 + 16)
            act.wait_ge(unit_used, u + (FU - 1))
            nc.scalar.activation(w_hi[:, s, :], raw_w[:, s, :], ACT.Copy).then_inc(ffn_hi, 1)

        def loads_before(u):
            return u // 2

        def ffn_hi_unit(u):
            split_hi((FU + u) % 2, u, loads_before(FU + u))

        ffn_hi_unit(0)
        for t in range(TT):
            normalise(t, u_acc[:, t, :], ln1_moments, t + 1)
            cond = 0 if t == 0 else 1
            for b in range(4):
                i = 4 * t + b
                act.wait_ge(turned2, i + 1)
                if t == 0 and b == 0:
                    act.wait_ge(folded, 5)
                if i >= 2:
                    act.wait_ge(h2_split, i - 1)
                for k in range(4):
                    kt = 4 * b + k
                    ins = nc.scalar.activation(lo(N_HT + (i % 2) * 512 + k * P, P),
                                               ps[:, 4 * (t % 2) + b, k * P:(k + 1) * P], ACT.Identity,
                                               bias=fold[:, SH, kt, cond:cond + 1],
                                               scale=fold[:, SC, kt, cond:cond + 1])
                ins.then_inc(h2_tmp, 1)

        def silu_block(slot):
            return nc.scalar.activation(halves(lo(F_SIL + slot * T, T)), ps[:, 0:2, 0:HALF], ACT.Silu)

        ffn_hi_unit(1)
        for b in range(2):
            if b:
                ffn_hi_unit(3)
            act.wait_ge(unit_used, FU + 2 * b + 1)
            if b == 0:
                act.wait_ge(x1_done, TT)
            silu_block(b).then_inc(silu_done, 1)
            ffn_hi_unit(2 + 2 * b)
        with act.Fori(1, FB // 2) as i:
            for b in range(2):
                u = PEEL - 6 + 3 * b
                s = (FU + u) % 2
                for j in range(2):
                    split_hi((s + j) % 2, i * 6 + (u + j), i * 3 + loads_before(FU + u + j))
                act.wait_ge(unit_used, i * 6 + (FU + u + 1))
                act.wait_ge(gated, i * 2 + (b - 1))
                silu_block(b).then_inc(silu_done, 1)
                split_hi(s, i * 6 + (u + 2), i * 3 + loads_before(FU + u + 2))
        ffn_hi_unit(3 * FB - 1)

        for t in range(TT):
            normalise(t, u_acc[:, t, :], moments, TT + t + 1)

    @block.vector
    def _(dve):
        steps = [0]

        def link(ins):
            steps[0] += 1
            ins.then_inc(dve_step, 1)
            dve.wait_ge(dve_step, steps[0])

        def stats(tile, at, blocks):
            for i in blocks:
                ins = nc.vector.bn_stats(at[:, 6 * i:6 * i + 6], tile[:, 512 * i:512 * i + 512])
            return ins

        def evac_turned(t):
            for b in range(4):
                i = 4 * t + b
                dve.wait_ge(turned, i + 1)
                nc.vector.tensor_copy(xT[:, 4 * b:4 * b + 4, t * P:(t + 1) * P],
                                      tiles(ps[:, 4 + b, :])).then_inc(turned_out, 1)

        def affine(t, tile, gain, shift, done, n):
            dve.wait_ge(normed, n)
            link(nc.vector.tensor_tensor(tile, tile, gain, ALU.mult))
            nc.vector.tensor_tensor(tile, tile, shift, ALU.add).then_inc(done, 1)

        def ln_in(t):
            dve.wait_ge(x_in[t % 3], 16 * (t // 3 + 1))
            link(stats(lo(S_X + (t % 3) * D, D), cols(C_STAT + 24 * (t % 2), 24), range(4)))
            nc.vector.bn_aggr(mv(TT + t, 0, 2), cols(C_STAT + 24 * (t % 2), 24)).then_inc(moments, 1)

        def add_bias(i, q, dst, src, done):
            bias = b_ada_col[:, i, 4 * q:4 * q + 4].unsqueeze(2).to_broadcast([P, 4, 2])
            nc.vector.tensor_tensor(dst, src, bias, ALU.add).then_inc(done, 1)

        def fold_norm(v_off, k, n):
            gain = vec(v_off + k, n).unsqueeze(2).to_broadcast([P, n, 2])
            shift = vec(v_off + KT + k, n).unsqueeze(2).to_broadcast([P, n, 2])
            one_sc = mod_col[:, SC, k:k + n]
            link(nc.vector.tensor_scalar(one_sc, one_sc, 1.0, None, ALU.add))
            nc.vector.tensor_tensor(fold[:, SC, k:k + n], one_sc, gain, ALU.mult)
            link(nc.vector.tensor_tensor(fold[:, SH, k:k + n], one_sc, shift, ALU.mult))
            nc.vector.tensor_tensor(fold[:, SH, k:k + n], fold[:, SH, k:k + n],
                                    mod_col[:, SH, k:k + n], ALU.add).then_inc(folded, 1)

        for g in range(2):
            for t in ((0, 1, 2), (3, 4))[g]:
                ln_in(t)
                if t not in (0, 3):
                    evac_turned(t - 1)
            evac_turned((2, 4)[g])
            for q in range(4):
                i = 4 * g + q
                dve.wait_ge(mod_turned, i + 1)
                add_bias(g, q, mod_col[:, g, 4 * q:4 * q + 4, :],
                         ps[:, 4 + i % 4, 0:8].rearrange("p (k c) -> p k c", c=2), mod_cols)
                if g == 1:
                    dve.wait_ge(mod_cols, i + 1)
                    fold_norm(V_LNIN, 4 * q, 4)

        def split_tile(src, k, done):
            link(nc.vector.tensor_copy(x_hi[:, k, :], src))
            nc.vector.tensor_tensor(x_lo[:, k, :], src, x_hi[:, k, :].bitcast(F32),
                                    ALU.subtract).then_inc(done, 1)

        for k in range(KT):
            dve.wait_ge(h_tmp, k + 1)
            split_tile(high[:, (k % 2) * T:(k % 2) * T + T], k, h_split)

        def ada_tiles(a, tiles_):
            for k in tiles_:
                i = KT * a + k
                w = high[:, H_RING + 512 * (i % ADA_SLOTS):H_RING + 512 * (i % ADA_SLOTS) + 512]
                dve.wait_ge(ada_in[i % ADA_SLOTS], 16 * (i // ADA_SLOTS + 1))
                if k == 0 and 1 <= a <= 12:
                    x, n = USES["adasum", a - 1, 0][0]
                    dve.wait_ge(filled[x], n + 1)
                elif k == 0 and a > 12:
                    dve.wait_ge(row_mm, a - 12)
                for c in range(2):
                    acc = high[:, H_ACC + 512 * c:H_ACC + 512 * c + 512]
                    s = cond_silu[:, k, c:c + 1]
                    if k == 0:
                        ins = nc.vector.tensor_scalar(acc, w, s, None, ALU.mult)
                    else:
                        if c == 0:
                            dve.wait_ge(ada_used, i)
                        ins = nc.vector.scalar_tensor_tensor(acc, w, s, acc, ALU.mult, ALU.add)
                ins.then_inc(ada_used, 1)

        def pool_tile(grp, j):
            w = WINDOWS[grp]
            jj = 2 * grp + j
            out = lo(L_POOLED + j * T, T)
            rc = lo(L_RC, T)
            pa, pb, pc = L_PA, L_PB, L_PC
            if jj >= 2:
                for x, k in USES["poolmm", grp - 1, 0]:
                    dve.wait_ge(filled[x], k + 1)
            if j == 0:
                dve.wait_ge(pool_in, 32 * (grp + 1))
            src, n, s, dst = lo(pa, PPR), PPR, 1, pb
            while s < w:
                n -= s
                link(nc.vector.tensor_tensor(lo(dst, n), src[:, 0:n], src[:, s:s + n], ALU.add))
                src, dst, s = lo(dst, n), (pc if dst == pb else pb), 2 * s
            at = PAD - w // 2
            link(nc.vector.tensor_tensor(out[:, 0:N_PROMPT], src[:, at:at + N_PROMPT],
                                         rc[:, 0:N_PROMPT], ALU.mult))
            nc.vector.tensor_tensor(out[:, 0:N_PROMPT], out[:, 0:N_PROMPT], lo(pa + PAD, N_PROMPT),
                                    ALU.subtract)
            grid = lo(pa + PPR, ROWS * PROW).rearrange("p (r c) -> p r c", r=ROWS)
            src, n, s, dst = grid, PROW, 1, pb
            while s < w:
                n -= s
                nxt = lo(dst, ROWS * PROW).rearrange("p (r c) -> p r c", r=ROWS)
                link(nc.vector.tensor_tensor(nxt[:, :, 0:n], src[:, :, 0:n], src[:, :, s:s + n], ALU.add))
                src, dst, s = nxt, (pc if dst == pb else pb), 2 * s
            run = lo(dst, ROWS * GRID_W).rearrange("p (r c) -> p r c", r=ROWS)
            link(nc.vector.tensor_copy(run[:, 0, :], src[:, 0, at:at + GRID_W]))
            for r in range(1, ROWS):
                link(nc.vector.tensor_tensor(run[:, r, :], run[:, r - 1, :], src[:, r, at:at + GRID_W],
                                             ALU.add))
            o2 = out[:, N_PROMPT:T].rearrange("p (r c) -> p r c", r=ROWS)
            up = min(w // 2 - 1, ROWS - 1)
            if up:
                nc.vector.tensor_copy(o2[:, ROWS - up:ROWS, :],
                                      run[:, ROWS - 1:ROWS, :].to_broadcast([P, up, GRID_W]))
            link(nc.vector.tensor_copy(o2[:, 0:ROWS - up, :], run[:, up:ROWS, :]))
            off = w // 2 + 1
            if off < ROWS:
                link(nc.vector.tensor_tensor(o2[:, off:ROWS, :], o2[:, off:ROWS, :],
                                             run[:, 0:ROWS - off, :], ALU.subtract))
            link(nc.vector.tensor_tensor(out[:, N_PROMPT:T], out[:, N_PROMPT:T], rc[:, N_PROMPT:T],
                                         ALU.mult))
            nc.vector.tensor_tensor(o2, o2, grid[:, :, PAD:PAD + GRID_W], ALU.subtract).then_inc(pooled, 1)

        for kind, a, b, uses in SCHEDULE:
            g = scan_index(a, b) if kind in ("gate", "cum", "score", "outer", "mix") else 0
            if kind == "ada":
                ada_tiles(a, (b,))
            elif kind == "adacol":
                x, k = uses[0]
                grp = a // 4
                slot = ADA[grp][2]
                dve.wait_ge(filled[x], k + 1)
                q = a % 4
                add_bias(2 + slot, q, mod_col[:, slot, 4 * q:4 * q + 4, :],
                         pair(x, 8).rearrange("p (k c) -> p k c", c=2), drained[x])
            elif kind == "gate":
                x, k = uses[0]
                dve.wait_ge(filled[x], k + 1)
                nc.vector.tensor_scalar(lo(L_LA, T), pair(x), 0.0, None, ALU.min).then_inc(gate_split, 1)
                dve.wait_ge(gate_split, g + 1)
                dve.wait_ge(softplus, g + 1)
                nc.vector.tensor_tensor(lo(L_LA, T), lo(L_LA, T), lo(L_E, T),
                                        ALU.subtract).then_inc(la_ready, 1)
            elif kind == "cum":
                x, k = uses[0]
                dve.wait_ge(filled[x], k + 1)
                at = CHUNK - 1 if b == 0 else 0
                bt = tiles(pair(x), CHUNK)
                link(nc.vector.tensor_copy(cols(C_BL, NCH).unsqueeze(2), bt[:, :, at:at + 1]))
                nc.vector.tensor_tensor(tiles(lo(L_E3, T), CHUNK),
                                        cols(C_BL, NCH).unsqueeze(2).to_broadcast([P, NCH, CHUNK]),
                                        bt, ALU.subtract).then_inc(bdiff, 1)
                dve.wait_ge(expb, g + 1)
                nc.vector.tensor_tensor(lo(L_QE, T), lo(L_Q, T), lo(L_E, T), ALU.mult).then_inc(qe_done, 1)
                dve.wait_ge(expd, g + 1)
                nc.vector.tensor_tensor(lo(L_E3, T), lo(L_K, T), lo(L_E3, T), ALU.mult).then_inc(kd_done, 1)
                dve.wait_ge(drained[x], k + 1)
                nc.vector.tensor_tensor(lo(L_KE, T), lo(L_K, T), lo(L_E, T), ALU.mult).then_inc(ke_done, 1)
            elif kind == "score":
                (xa, ka), (xb, kb) = uses
                dve.wait_ge(filled[xa], ka + 1)
                dve.wait_ge(filled[xb], kb + 1)
                link(nc.vector.memset(lo(L_E3, T), 0.0))
                mask = tri(b).bitcast(U32).unsqueeze(1).to_broadcast([P, TT, P])
                nc.vector.copy_predicated(tiles(lo(L_E3, T)), mask, tiles(pair(xa))).then_inc(drained[xa], 1)
            elif kind == "outer":
                pr, sa = chunk_order(b)
                order = pr + sa[:-1]

                def st(i):
                    return lo(L_ST + 256 * i, 256)

                if g:
                    dve.wait_ge(state_out, 16 * g)
                dve.wait_ge(state_in, 16 * (g + 1))
                for i, c in enumerate(order):
                    x, k = uses[i // 4]
                    if i % 4 == 0:
                        dve.wait_ge(filled[x], k + 1)
                    at = outer_col(i)
                    up = pair(x, 1024)[:, at:at + 256]
                    decay = cols(C_DEC + c, 1)
                    if i == 0:
                        ins = nc.vector.tensor_copy(st(0), up)
                    elif i == 1:
                        ins = nc.vector.scalar_tensor_tensor(st(FINAL), st(0), decay, up, ALU.mult, ALU.add)
                    else:
                        ins = nc.vector.scalar_tensor_tensor(st(i), st(i - 1), decay, up, ALU.mult, ALU.add)
                    if i == 1:
                        ins.then_inc(final_state, 1)
                    elif i % 4 == 3 or i == len(order) - 1:
                        ins.then_inc(drained[x], 1)
                        dve.wait_ge(drained[x], k + 1)
                    else:
                        link(ins)
            elif kind == "mix":
                for dv, (x, k) in enumerate(uses):
                    o = lo(L_O + dv * T, T)
                    dve.wait_ge(filled[x], k + 1)
                    if b == 0:
                        if a:
                            dve.wait_ge(o_out, 16 * a)
                        nc.vector.tensor_copy(o, pair(x)).then_inc(drained[x], 1)
                    else:
                        xx, kk = USES["mix", a, 0][dv]
                        dve.wait_ge(drained[xx], kk + 1)
                        nc.vector.tensor_tensor(o, o, pair(x), ALU.add).then_inc(drained[x], 1)
            elif kind == "norm":
                dve.wait_ge(rms_done, a + 1)
                for dv in range(2):
                    o = lo(L_O + dv * T, T)
                    nc.vector.scalar_tensor_tensor(o, o, vec(V_NORM + 2 * a + dv, 1), lo(L_LA, T),
                                                   ALU.mult, ALU.mult).then_inc(o_normed, 1)
            elif kind == "pool":
                n = [i for i, p in enumerate(PLAN) if p[:3] == ("p", a, b)][0]
                dve.wait_ge(zin_evac, n + 1)
                pool_tile(a, b)

        n_in = [0, 0]
        dve.wait_ge(unit_used, N_IN)
        for i in range(KT):
            kt = KG_ORDER[i // 4] * 4 + i % 4
            base = W_MIX + (i % 2) * 2 * T
            n_in[i % 2] += 32 if kt < 8 else 16
            dve.wait_ge(mix_in[i % 2], n_in[i % 2])
            if kt < 8:
                link(nc.vector.tensor_tensor(lo(base, T), lo(base, T), lo(base + T, T), ALU.mult))
            split_tile(lo(base, T), kt, mix_split)

        stat1 = lo(W_STAT, 24 * TT).rearrange("p (t c) -> p t c", t=TT)
        for nb in range(4):
            base = W_GATE[nb % 2]
            dve.wait_ge(gate_in[nb % 2], 80 * (nb // 2 + 1))
            for i in range(2):
                link(nc.vector.tensor_tensor(lo(base + 512 * i, 512), lo(base + 512 * i, 512),
                                             lo(base + 1024, 512), ALU.add))
            for t in range(TT):
                blk = u_acc[:, t, nb * 512:nb * 512 + 512]
                dve.wait_ge(x_normed, t + 1)
                nc.vector.tensor_tensor(blk, blk, lo(base + 1536, 512), ALU.mult).then_inc(res_gain, 1)
            for t in range(TT):
                blk = u_acc[:, t, nb * 512:nb * 512 + 512]
                dve.wait_ge(res_gain, TT * nb + t + 1)
                ins = nc.vector.tensor_tensor(blk, blk, lo(base + 2048, 512), ALU.add)
            link(ins)
            ada_tiles(12 + nb, range(KT))
            for t in range(TT):
                i = TT * nb + t
                gate = lo(base + (0 if t == 0 else 512), 512)
                blk = u_acc[:, t, nb * 512:nb * 512 + 512]
                acc = ps[:, i % 7, :]
                if t < TT - 1:
                    dve.wait_ge(out_filled, (TT - 1) * nb + t + 1)
                else:
                    dve.wait_ge(unit_used, N_IN + 4 * nb + 4)
                link(nc.vector.tensor_tensor(acc, acc, gate, ALU.mult))
                nc.vector.scalar_tensor_tensor(blk, blk, ALPHA, acc, ALU.mult, ALU.add).then_inc(out_evac, 1)
                dve.wait_ge(out_evac, i + 1)
                ins = stats(u_acc[:, t, :], stat1[:, t], [nb])
                if nb == 3:
                    link(ins)
                    nc.vector.bn_aggr(mv(t, 0, 2), stat1[:, t]).then_inc(ln1_moments, 1)

        xa, ka = USES["adacol", 11, 0][0]
        dve.wait_ge(drained[xa], ka + 1)
        fold_norm(V_LN1, 0, KT)
        for t in range(TT):
            for b in range(4):
                i = 4 * t + b
                dve.wait_ge(h2_tmp, i + 1)
                src = tiles(lo(N_HT + (i % 2) * 512, 512))
                hi = x_hi[:, 4 * b:4 * b + 4, t * P:(t + 1) * P]
                link(nc.vector.tensor_copy(hi, src))
                nc.vector.tensor_tensor(x_lo[:, 4 * b:4 * b + 4, t * P:(t + 1) * P], src,
                                        hi.bitcast(F32), ALU.subtract).then_inc(h2_split, 1)
        dve.wait_ge(ln_rows_in, 32)
        for t in range(TT):
            affine(t, u_acc[:, t, :], lo(N_VECB, D), lo(N_VECB + D, D), x1_done, TT + t + 1)

        def hidden(slot, after):
            hf = lo(F_HF, T)
            nc.vector.tensor_tensor(hf.rearrange("p (b c) -> p b c", b=2),
                                    lo(F_SIL + slot * T, T).rearrange("p (b c) -> p b c", b=2),
                                    ps[:, 2:4, 0:HALF], ALU.mult).then_inc(gated, 1)
            dve.wait_ge(gated, after + 1)
            nc.vector.tensor_copy(hid[:, slot, 0, :], hf).then_inc(hid_hi, 1)
            dve.wait_ge(hid_hi, after + 1)
            nc.vector.tensor_tensor(hid[:, slot, 1, :], hf, hid[:, slot, 0, :].bitcast(F32),
                                    ALU.subtract).then_inc(hid_ready, 1)

        def add_down(tiles_before, unit_done, first=False):
            for i in range(4 * TT):
                t, nb = i // 4, i % 4
                blk = u_acc[:, t, nb * 512:nb * 512 + 512]
                if i < 4 * TT - 1:
                    dve.wait_ge(down_tile, tiles_before + (i + 1))
                else:
                    dve.wait_ge(unit_used, unit_done)
                src = ps[:, 4 + i % 4, :]
                if first:
                    nc.vector.tensor_copy(blk, src).then_inc(down_evac, 1)
                else:
                    nc.vector.tensor_tensor(blk, blk, src, ALU.add).then_inc(down_evac, 1)

        dve.wait_ge(row_out, 16 * 8)
        dve.wait_ge(silu_done, 1)
        dve.wait_ge(unit_used, FU + 2)
        hidden(0, 0)
        dve.wait_ge(x1_out, 16 * TT)
        add_down(0, FU + PEEL, first=True)
        dve.wait_ge(silu_done, 2)
        hidden(1, 1)
        with dve.Fori(1, FB // 2) as i:
            for b in range(2):
                dve.wait_ge(down_evac, i * 40 + (20 * b - 20))
                add_down(i * 38 + 19 * (b - 1), i * 6 + (FU + PEEL - 6 + 3 * b + 3))
                dve.wait_ge(silu_done, i * 2 + (b + 1))
                hidden(b, i * 2 + b)
        dve.wait_ge(down_evac, 20 * (FB - 1))
        add_down(19 * (FB - 1), FU + 3 * FB)

        dve.wait_ge(tail_rows_in, 16 * 5)
        nc.vector.tensor_tensor(lo(E_GATE, D), lo(E_GATE, D), lo(E_X, D), ALU.add)
        nc.vector.tensor_tensor(lo(E_GATE + D, D), lo(E_GATE + D, D), lo(E_X, D), ALU.add).then_inc(gates2, 1)
        dve.wait_ge(gates2, 1)
        dve.wait_ge(down_evac, 20 * FB)
        for t in range(TT):
            tile = u_acc[:, t, :]
            link(nc.vector.tensor_tensor(tile, tile, lo(E_GATE + (0 if t == 0 else D), D), ALU.mult))
            dve.wait_ge(x1_in, 16 * (t + 1))
            nc.vector.scalar_tensor_tensor(tile, lo(E_X, D), ALPHA, tile, ALU.mult, ALU.add).then_inc(y_sum, 1)
            dve.wait_ge(y_sum, t + 1)
            link(stats(tile, cols(C_STAT + 24 * (t % 2), 24), range(4)))
            nc.vector.bn_aggr(mv(t, 0, 2), cols(C_STAT + 24 * (t % 2), 24)).then_inc(moments, 1)
            if t:
                affine(t - 1, u_acc[:, t - 1, :], raw_w[:, 0, :], raw_w[:, 1, :], y_done, 2 * TT + t)
        affine(TT - 1, u_acc[:, TT - 1, :], raw_w[:, 0, :], raw_w[:, 1, :], y_done, 3 * TT)

    @block.tensor
    def _(pe):
        mm = nc.tensor.matmul
        pe.wait_ge(consts_in, 32)
        pe.wait_ge(cond_ready, 1)

        def turn_x(t):
            pe.wait_ge(normed, t + 1)
            for b in range(4):
                if t:
                    pe.wait_ge(turned_out, 4 * t + b - 3)
                for k in range(4):
                    c = (4 * b + k) * P
                    ins = nc.tensor.transpose(ps[:, 4 + b, k * P:(k + 1) * P],
                                              lo(S_X + (t % 3) * D + c, P), ident)
                ins.then_inc(turned, 1)

        for g in range(2):
            for k in range(KT):
                r = KT * g + k
                if g == 1 and k == 0:
                    pe.wait_ge(mod_rows, 4)
                for half in range(2):
                    slot = (2 * r + half) % 4
                    pe.wait_ge(half_in[slot], 16 * (r // 2 + 1))
                    for q in range(2):
                        ins = mm(ps[0:2, 2 * half + q, :], cond_silu[:, k, :],
                                 raw_half[:, slot, q * 512:q * 512 + 512], start=k == 0, stop=k == KT - 1)
                    ins.then_inc(mod_used, 1)
                if r in X_TURNS:
                    if X_TURNS.index(r) == 3:
                        pe.wait_ge(mod_cols, 4)
                    turn_x(X_TURNS.index(r))
            if g == 1:
                pe.wait_ge(turned_out, 4 * TT)
            for q in range(4):
                i = 4 * g + q
                pe.wait_ge(mod_rows, i + 1)
                if g == 0:
                    pe.wait_ge(turned_out, 4 * 3)
                if i >= 4:
                    pe.wait_ge(mod_cols, i - 3)
                for k in range(4):
                    c = 2048 + 512 * (q % 2) + k * P
                    ins = nc.tensor.transpose(ps[:, 4 + i % 4, 2 * k:2 * k + 2], high[0:2, c:c + P],
                                              ident[0:2, 0:2])
                ins.then_inc(mod_turned, 1)
        pe.wait_ge(mod_cols, 8)

        def three_passes(s, k, banks, first, last):
            wh = w_hi[:, s, k * P:(k + 1) * P]
            wl = w_lo[:, s, k * P:(k + 1) * P]
            for w, x, begin, end in ((wh, x_hi, first, False), (wh, x_lo, False, False),
                                     (wl, x_hi, False, last)):
                for half in range(2):
                    ins = mm(ps[:, banks + half, 0:HALF], w, x[:, k, half * HALF:(half + 1) * HALF],
                             start=begin, stop=end)
            return ins

        def pair_mm(x, n, c, w, rhs, start, stop, **kw):
            return mm(pair(x, 1024)[:, c:c + n], w, rhs, start=start, stop=stop, **kw)

        def take(x, k):
            if k:
                pe.wait_ge(drained[x], k)

        for kind, a, b, uses in SCHEDULE:
            g = scan_index(a, b) if kind in ("gate", "cum", "score", "outer", "mix") else 0
            if kind == "main":
                s = a % 2
                if b == 0:
                    pe.wait_ge(split_done, a + 1)
                    if a >= 2:
                        pe.wait_ge(zin_evac, a - 1)
                for k in range(4 * b, 4 * b + 4):
                    if a == 0:
                        pe.wait_ge(h_split, k + 1)
                    ins = three_passes(s, k, 2 * s, k == 0, k == KT - 1)
                if b == 3:
                    ins.then_inc(unit_used, 1)
            elif kind == "vT":
                x, k = uses[0]
                n = [i for i, p in enumerate(PLAN) if p[:3] == ("v", a, b)][0]
                pe.wait_ge(zin_evac, n + 1)
                take(x, k)
                src = L_STAGE + (STAGE_AT["v", a, b] % 2) * T
                for t in range(TT):
                    ins = nc.tensor.transpose(pair(x)[:, t * P:(t + 1) * P], lo(src + t * P, P), ident)
                ins.then_inc(filled[x], 1)
            elif kind == "gate":
                x, k = uses[0]
                pe.wait_ge(zin_evac, 1)
                pe.wait_ge(ones_row, 1)
                pe.wait_ge(wa_in, 16 * (a + 1))
                take(x, k)
                for t in range(TT):
                    ins = pair_mm(x, P, t * P, low[0:K_ARR, L_AT + t * P:L_AT + (t + 1) * P],
                                  low[0:K_ARR, L_WA + b * P:L_WA + (b + 1) * P], True, True)
                ins.then_inc(filled[x], 1)
            elif kind == "cum":
                x, k = uses[0]
                pe.wait_ge(la_ready, g + 1)
                take(x, k)
                for t in range(TT):
                    ins = pair_mm(x, P, t * P, lo(L_LA + t * P, P), tri(b), True, True)
                ins.then_inc(filled[x], 1)
            elif kind == "score":
                (xa, ka), (xb, kb) = uses
                pe.wait_ge(kd_done, g + 1)
                take(xb, kb)
                for t in range(TT):
                    ins = nc.tensor.transpose(pair(xb)[:, t * P:(t + 1) * P], lo(L_E3 + t * P, P), ident)
                ins.then_inc(filled[xb], 1)
                pe.wait_ge(ke_done, g + 1)
                take(xa, ka)
                for t in range(TT):
                    ins = pair_mm(xa, P, t * P, lo(L_KE + t * P, P), lo(L_QE + t * P, P), True, True)
                ins.then_inc(filled[xa], 1)
            elif kind == "outer":
                xs, ks = USES["score", a, b][1]
                pe.wait_ge(drained[xs], ks + 1)
                for xv, kv in (USES["vT", a, 0][0], USES["vT", a, 1][0]):
                    pe.wait_ge(drained[xv], kv + 1)
                pr, sa = chunk_order(b)
                order = pr + sa[:-1]
                for i, c in enumerate(order):
                    x, k = uses[i // 4]
                    if i % 4 == 0:
                        take(x, k)
                    r = CHUNK * (c % 2)
                    t = c // 2
                    ins = pair_mm(x, 256, outer_col(i), low[r:r + CHUNK, L_LA + t * P:L_LA + (t + 1) * P],
                                  low[r:r + CHUNK, L_V + t * DV:L_V + (t + 1) * DV], True, True)
                    if i % 4 == 3 or i == len(order) - 1:
                        ins.then_inc(filled[x], 1)
            elif kind == "mix":
                slots = state_slot(b)
                xs, ks = USES["score", a, b][0]
                pe.wait_ge(drained[xs], ks + 1)
                for xo, ko in USES["outer", a, b]:
                    pe.wait_ge(drained[xo], ko + 1)
                for dv, (x, k) in enumerate(uses):
                    take(x, k)
                    for t in range(TT):
                        inter = [c for c in (2 * t, 2 * t + 1) if c in slots]
                        ins = pair_mm(x, P, t * P, lo(L_V + t * DV + dv * P, P), lo(L_E3 + t * P, P),
                                      True, False, skip_group_check=True)
                        for c in inter:
                            ins = pair_mm(x, CHUNK, c * CHUNK, lo(L_ST + slots[c] * 256 + dv * P, P),
                                          lo(L_QE + c * CHUNK, CHUNK), False, c == inter[-1],
                                          skip_group_check=True)
                    ins.then_inc(filled[x], 1)
            elif kind == "norm":
                x, k = uses[0]
                pe.wait_ge(squared, a + 1)
                take(x, k)
                for c, n in ((0, 512), (512, T - 512)):
                    for dv in range(2):
                        ins = pair_mm(x, n, c, ones, lo(L_E + dv * T + c, n), dv == 0, dv == 1)
                ins.then_inc(filled[x], 1)
            elif kind == "poolmm":
                pe.wait_ge(pooled, 2 * a + 2)
                pe.wait_ge(pool_in, 32 * (a + 1))
                for blk, (x, k) in enumerate(uses):
                    take(x, k)
                    for c, n in ((0, 512), (512, T - 512)):
                        for c2 in range(2):
                            ins = pair_mm(x, n, c, lo(L_WP + c2 * 256 + blk * P, P),
                                          lo(L_POOLED + c2 * T + c, n), c2 == 0, c2 == 1)
                    ins.then_inc(filled[x], 1)
            elif kind == "adasum":
                x, k = uses[0]
                pe.wait_ge(ada_used, KT * (a + 1))
                take(x, k)
                for c in range(2):
                    ins = mm(pair(x, 512)[0:2, :], cols(C_IND + 2 * c, 2), high[:, H_ACC + 512 * c:H_ACC + 512 * c + 512],
                             start=c == 0, stop=c == 1)
                ins.then_inc(filled[x], 1)
            elif kind == "adacol":
                x, k = uses[0]
                xs, ks = USES["adasum", a, 0][0]
                pe.wait_ge(drained[xs], ks + 1)
                take(x, k)
                for kk in range(4):
                    ins = nc.tensor.transpose(pair(x, 8)[:, 2 * kk:2 * kk + 2],
                                              high[0:2, H_ROW + kk * P:H_ROW + (kk + 1) * P], ident[0:2, 0:2])
                ins.then_inc(filled[x], 1)

        pe.wait_ge(zin_evac, N_IN)
        for x in range(2):
            pe.wait_ge(drained[x], FILLS[x])

        def ada_rows(a):
            pe.wait_ge(ada_used, KT * (a + 1))
            if a > 12:
                pe.wait_ge(ada_row, a - 12)
            for c in range(2):
                ins = mm(ps[0:2, 7, :], cols(C_IND + 2 * c, 2), high[:, H_ACC + 512 * c:H_ACC + 512 * c + 512],
                         start=c == 0, stop=c == 1)
            ins.then_inc(row_mm, 1)

        for nb in range(4):
            for kg in range(4):
                u = N_IN + 4 * nb + kg
                s = u % 2
                pe.wait_ge(split_done, u + 1)
                for t in range(TT):
                    i = TT * nb + t
                    if kg == 0 and i >= 7:
                        pe.wait_ge(out_evac, i - 6)
                    for k in range(4):
                        kt = KG_ORDER[kg] * 4 + k
                        if nb == 0:
                            pe.wait_ge(mix_split, 4 * kg + k + 1)
                        rh = w_hi[:, s, k * 512:(k + 1) * 512]
                        rl = w_lo[:, s, k * 512:(k + 1) * 512]
                        xh = x_hi[:, kt, t * P:(t + 1) * P]
                        xl = x_lo[:, kt, t * P:(t + 1) * P]
                        begin, end = kg == 0 and k == 0, kg == 3 and k == 3
                        mm(ps[:, i % 7, :], xh, rh, start=begin, stop=False)
                        mm(ps[:, i % 7, :], xh, rl, start=False, stop=False)
                        ins = mm(ps[:, i % 7, :], xl, rh, start=False, stop=end)
                    if kg == 3 and t < TT - 1:
                        ins.then_inc(out_filled, 1)
                    elif t == TT - 1:
                        ins.then_inc(unit_used, 1)
            ada_rows(12 + nb)

        pe.wait_ge(out_evac, OUT_ACC)
        for t in range(TT):
            pe.wait_ge(normed, TT + t + 1)
            if t == 1:
                pe.wait_ge(ada_row, 4)
            for b in range(4):
                if t >= 2:
                    pe.wait_ge(h2_tmp, 4 * (t - 2) + b + 1)
                for k in range(4):
                    c = (4 * b + k) * P
                    ins = nc.tensor.transpose(ps[:, 4 * (t % 2) + b, k * P:(k + 1) * P],
                                              u_acc[:, t, c:c + P], ident)
                ins.then_inc(turned2, 1)
        pe.wait_ge(h2_split, 4 * TT)

        def hidden_block(s, banks):
            for k in range(KT):
                ins = three_passes(s, k, banks, k == 0, k == KT - 1)
            ins.then_inc(unit_used, 1)

        def down_block(s, slot, evac_before):
            for i in range(4 * TT):
                t, nb = i // 4, i % 4
                if evac_before is not None:
                    pe.wait_ge(down_evac, evac_before + (i - 3))
                elif i >= 4:
                    pe.wait_ge(down_evac, i - 3)
                h_hi = hid[:, slot, 0, t * P:(t + 1) * P]
                h_lo = hid[:, slot, 1, t * P:(t + 1) * P]
                d_hi = w_hi[:, s, nb * 512:nb * 512 + 512]
                d_lo = w_lo[:, s, nb * 512:nb * 512 + 512]
                out = ps[:, 4 + i % 4, :]
                mm(out, h_hi, d_hi, start=True, stop=False)
                mm(out, h_hi, d_lo, start=False, stop=False)
                mm(out, h_lo, d_hi, start=False, stop=True).then_inc(
                    down_tile if i < 4 * TT - 1 else unit_used, 1)

        for b in range(2):
            pe.wait_ge(split_done, FU + 2 * b + 1)
            if b:
                pe.wait_ge(silu_done, 1)
            hidden_block((FU + 2 * b) % 2, 0)
            pe.wait_ge(split_done, FU + 2 * b + 2)
            if b:
                pe.wait_ge(gated, 1)
            hidden_block((FU + 2 * b + 1) % 2, 2)
        pe.wait_ge(split_done, FU + PEEL)
        pe.wait_ge(hid_ready, 1)
        down_block((FU + 4) % 2, 0, None)
        with pe.Fori(1, FB // 2) as i:
            for b in range(2):
                u = FU + PEEL + 3 * b
                pe.wait_ge(split_done, i * 6 + (u - 6 + 1))
                pe.wait_ge(silu_done, i * 2 + b)
                hidden_block(u % 2, 0)
                pe.wait_ge(split_done, i * 6 + (u - 6 + 2))
                pe.wait_ge(gated, i * 2 + b)
                hidden_block((u + 1) % 2, 2)
                pe.wait_ge(split_done, i * 6 + (u - 6 + 3))
                pe.wait_ge(hid_ready, i * 2 + b)
                down_block((u + 2) % 2, (b + 1) % 2, i * 40 + (20 * b - 20))
        last = FU + 3 * FB - 1
        pe.wait_ge(split_done, last + 1)
        pe.wait_ge(hid_ready, FB)
        down_block(last % 2, (FB - 1) % 2, 20 * (FB - 1))

    block.__exit__(None, None, None)


def shape_constants():
    c = np.zeros((P, C_VEC), np.float32)
    i = np.arange(P)
    c[:, C_IDENT:C_IDENT + P] = np.eye(P)
    same = (i[:, None] // CHUNK) == (i[None, :] // CHUNK)
    c[:, C_TRI:C_TRI + P] = (same & (i[:, None] <= i[None, :])) / GATE_TEMP
    c[:, C_TRI + P:C_TRI + 2 * P] = (same & (i[:, None] >= i[None, :])) / GATE_TEMP
    c[:, C_ONES:C_ONES + P] = 1.0
    c[:, C_IND] = 1.0
    c[:, C_IND + 3] = 1.0
    c[:, C_EPS] = EPS

    def size(n, w):
        j = np.arange(n)
        return np.clip(j - w // 2 + w, 0, n) - np.clip(j - w // 2, 0, n)

    r = np.zeros((len(WINDOWS), T), np.float32)
    for g, w in enumerate(WINDOWS):
        r[g, :N_PROMPT] = 1.0 / size(N_PROMPT, w)
        r[g, N_PROMPT:] = (1.0 / (size(ROWS, w)[:, None] * size(GRID_W, w)[None, :])).ravel()
    return c, r


def kernel(x_prompt, x_sample, state_gla, c, c_ctx, ln_in_g, ln_in_b, w_ada, b_ada, w_in, w_a2, b_a,
           gla_norm_g, w_pool, pool_scale, w_out, ln1_g, ln1_b, w_gu, w_down, ln2_g, ln2_b):
    import concourse.bacc as bacc
    from concourse.bass_utils import run_bass_kernel_spmd

    (x_prompt, x_sample, state_gla, c, c_ctx, ln_in_g, ln_in_b, w_ada, b_ada, w_in, w_a2, b_a, gla_norm_g,
     w_pool, pool_scale, w_out, ln1_g, ln1_b, w_gu, w_down, ln2_g, ln2_b) = (
        np.asarray(a) for a in (x_prompt, x_sample, state_gla, c, c_ctx, ln_in_g, ln_in_b, w_ada, b_ada,
                                w_in, w_a2, b_a, gla_norm_g, w_pool, pool_scale, w_out, ln1_g, ln1_b,
                                w_gu, w_down, ln2_g, ln2_b))

    def col(v):
        return v.reshape(-1, P).T

    def blocks(w):
        return w.reshape(KT, P, -1, P).transpose(2, 1, 0, 3).reshape(-1, P, UNIT)

    b6 = b_ada[0].reshape(6, D)
    consts, rcnt = shape_constants()
    vecs = np.concatenate(
        [col(gla_norm_g[0]), col(pool_scale[0]), col(ln_in_g), col(ln_in_b), col(ln1_g[0]), col(ln1_b[0]),
         col(b6[1]), col(b6[0]), col(b6[4]), col(b6[3]),
         np.stack([col(c_ctx), col(c[0])], axis=2).reshape(P, 2 * KT)], axis=1)
    rows = np.stack([ln_in_g, ln_in_b, ln1_g[0], ln1_b[0], ln2_g[0], ln2_b[0], b6[2], b6[5]])
    wa2 = np.zeros((K_ARR, 2, KEYW), np.float32)
    wa2[0:RANK, 0], wa2[RANK:2 * RANK, 1] = w_a2[0, 0], w_a2[0, 1]
    wa2[2 * RANK] = b_a[0]
    gu = w_gu[0].reshape(D, 2, FB, P).transpose(0, 2, 1, 3).reshape(D, 2 * D_FF)
    arrays = {
        "x_all": np.concatenate([x_prompt[0], x_sample[0]], axis=0),
        "state_gla": state_gla[0, :, 0],
        "w_ada": w_ada[0],
        "w_in_b": np.concatenate([blocks(w_in[0][:, at:at + P]) for _, _, _, at in PLAN], axis=0),
        "wa2": wa2,
        "w_pool_l": w_pool[0].reshape(4, 2, P, GROUPW).transpose(0, 2, 1, 3),
        "w_out": w_out[0],
        "w_gu_b": blocks(gu),
        "w_down": w_down[0],
        "consts": consts,
        "vecs": vecs,
        "rcnt": rcnt,
        "rows": rows,
    }
    arrays = {n: np.ascontiguousarray(a) for n, a in arrays.items()}
    nc = bacc.Bacc("TRN2", target_bir_lowering=False, num_devices=1)
    args = {n: nc.dram_tensor(n, a.shape, F32, kind="ExternalInput").ap() for n, a in arrays.items()}
    args["y_all"] = nc.dram_tensor("y_all", (T, D), F32, kind="ExternalOutput").ap()
    args["new_state"] = nc.dram_tensor("new_state", (2, HEADS, DK, DV), F32, kind="ExternalOutput").ap()
    backbone(nc, **args)
    got = run_bass_kernel_spmd(nc, [arrays], core_ids=[0]).results[0]
    y, state = got["y_all"], got["new_state"]
    return y[None, :N_PROMPT], y[None, N_PROMPT:], state[None, :, None]
```
